# Optimizing a Trainium2 kernel written in Bass

```python
import math
import jax, jax.numpy as jnp
from jax import lax
import numpy as np

D_MODEL = 1024
BATCH = 1
SEQ = 1024
DEPTH = 2

GRID_W = 64
CTX_LEN = 256
MIX_WIDTH = D_MODEL
F_GROUPS = 4
F_CH = MIX_WIDTH // 2 // F_GROUPS
F_WIDTH = F_GROUPS * F_CH
H_DIFF = 4
DH = MIX_WIDTH // 2 // H_DIFF // 2
DV = 2 * DH
QK_WIDTH = H_DIFF * 2 * DH
ATT_WIDTH = H_DIFF * DV
F0 = 0
Q0 = F0 + F_WIDTH
K0 = Q0 + QK_WIDTH
V0 = K0 + QK_WIDTH
G0 = V0 + ATT_WIDTH
EVEN_IN = G0 + MIX_WIDTH
CONV_WIDTH = MIX_WIDTH
CONV_K = 3
ODD_IN = 4 * CONV_WIDTH
N_EVEN = (DEPTH + 1) // 2
N_ODD = DEPTH // 2
ROPE_BASE = 10000.0
Q_BLOCK = 128
EPS = 1e-6
ATTN_SCALE = DH ** -0.5


def rms_norm(x, g):
    x32 = x.astype(jnp.float32)
    y = x32 * lax.rsqrt(jnp.mean(x32 * x32, axis=-1, keepdims=True) + EPS)
    return (y * g.astype(jnp.float32)).astype(x.dtype)

def ada_params(cvec, w, b):
    m = jax.nn.silu(cvec) @ w + b
    return jnp.split(m, 3, axis=-1)

def modulate(x, g, shift, scale):
    return rms_norm(x, g) * (1.0 + scale) + shift

def need_ctx_after(i):
    return any(j % 2 == 0 for j in range(i + 1, DEPTH))

def lambda_init_fn(layer_idx):
    return 0.8 - 0.6 * math.exp(-0.3 * layer_idx)

def axial_rope_tables(rows):
    pos_r = jnp.repeat(jnp.arange(rows, dtype=jnp.float32), GRID_W)
    pos_c = jnp.tile(jnp.arange(GRID_W, dtype=jnp.float32), rows)
    half = DH // 2
    freqs = ROPE_BASE ** (-jnp.arange(0, half, 2, dtype=jnp.float32) / half)
    ang_r = pos_r[:, None] * freqs
    ang_c = pos_c[:, None] * freqs
    return (jnp.cos(ang_r), jnp.sin(ang_r), jnp.cos(ang_c), jnp.sin(ang_c))

def _rotate(x, cos, sin):
    x1, x2 = jnp.split(x, 2, axis=-1)
    return jnp.concatenate([x1 * cos - x2 * sin, x1 * sin + x2 * cos], axis=-1)

def apply_axial_rope(x, tabs):
    cos_r, sin_r, cos_c, sin_c = [t[None, :, None, None, :].astype(x.dtype) for t in tabs]
    xr, xc = jnp.split(x, 2, axis=-1)
    return jnp.concatenate([_rotate(xr, cos_r, sin_r), _rotate(xc, cos_c, sin_c)], axis=-1)

def fourier_mix(u):
    b, n, _ = u.shape
    u32 = u.reshape(b, n, F_GROUPS, F_CH).astype(jnp.float32)
    f = jnp.fft.fftn(u32, axes=(1, 3), norm="ortho").real
    return f.reshape(b, n, F_WIDTH).astype(u.dtype)

def split_kv(kv, k_g):
    b, n, _ = kv.shape
    k = rms_norm(kv[..., :QK_WIDTH].reshape(b, n, H_DIFF, 2, DH), k_g)
    v = kv[..., QK_WIDTH:].reshape(b, n, H_DIFF, DV)
    return k, v

def split_qkv(proj, q_g, k_g):
    b, n, _ = proj.shape
    q = rms_norm(proj[..., Q0:K0].reshape(b, n, H_DIFF, 2, DH), q_g)
    k, v = split_kv(proj[..., K0:G0], k_g)
    return q, k, v

def diff_attention(q, k, v, lam):
    b, n = q.shape[:2]
    nblk = n // Q_BLOCK
    qb = q.reshape(b, nblk, Q_BLOCK, H_DIFF, 2, DH).swapaxes(0, 1)

    def one_block(qblk):
        s = jnp.einsum('bqhmd,bkhmd->bhmqk', qblk, k,
                       preferred_element_type=jnp.float32) * ATTN_SCALE
        p = jax.nn.softmax(s, axis=-1)
        a = p[:, :, 0] - lam * p[:, :, 1]
        return jnp.einsum('bhqk,bkhv->bqhv', a.astype(v.dtype), v)

    o = lax.map(one_block, qb)
    return o.swapaxes(0, 1).reshape(b, n, H_DIFF, DV)

def even_output(proj, attn_o, subln_g, lam_init, w_out):
    b, n, _ = proj.shape
    fo = fourier_mix(proj[..., F0:Q0])
    ao = (rms_norm(attn_o, subln_g) * (1.0 - lam_init)).reshape(b, n, ATT_WIDTH)
    y = jnp.concatenate([fo, ao], axis=-1) * jax.nn.silu(proj[..., G0:])
    return y @ w_out

def short_conv_mixer(proj, conv_w, w_out):
    bg, cg, xt, g = jnp.split(proj, 4, axis=-1)
    u = cg * xt
    n = u.shape[1]
    pad = CONV_K // 2
    up = jnp.pad(u, ((0, 0), (pad, pad), (0, 0)))
    conv = sum(conv_w[t] * up[:, t:t + n] for t in range(CONV_K))
    return (bg * conv * jax.nn.silu(g)) @ w_out

def first_inputs(seed: int = 0) -> dict:
    key = jax.random.key(seed)
    ks = jax.random.split(key, 20)
    f32 = jnp.float32
    D = D_MODEL
    nrm = lambda k, shape, s: (jax.random.normal(k, shape, f32) * s)
    return {
        "x": nrm(ks[0], (BATCH, SEQ, D), 1.0),
        "c": nrm(ks[1], (BATCH, D), 1.0),
        "ctx": nrm(ks[2], (BATCH, CTX_LEN, D), 1.0),
        "c_ctx": nrm(ks[3], (D,), 1.0),
        "norm_g": 1.0 + nrm(ks[4], (DEPTH, D), 0.02),
        "ada_w": nrm(ks[5], (DEPTH, D, 3 * D), D ** -0.5),
        "ada_b": nrm(ks[6], (DEPTH, 3 * D), 0.01),
        "even_w_in": nrm(ks[7], (N_EVEN, D, EVEN_IN), D ** -0.5),
        "even_q_norm": 1.0 + nrm(ks[8], (N_EVEN, DH), 0.02),
        "even_k_norm": 1.0 + nrm(ks[9], (N_EVEN, DH), 0.02),
        "even_lambda_q1": nrm(ks[10], (N_EVEN, DH), 0.1),
        "even_lambda_k1": nrm(ks[11], (N_EVEN, DH), 0.1),
        "even_lambda_q2": nrm(ks[12], (N_EVEN, DH), 0.1),
        "even_lambda_k2": nrm(ks[13], (N_EVEN, DH), 0.1),
        "even_subln": 1.0 + nrm(ks[14], (N_EVEN, DV), 0.02),
        "even_w_out": nrm(ks[15], (N_EVEN, MIX_WIDTH, D), MIX_WIDTH ** -0.5),
        "odd_w_in": nrm(ks[16], (N_ODD, D, ODD_IN), D ** -0.5),
        "odd_conv_w": nrm(ks[17], (N_ODD, CONV_K, CONV_WIDTH), CONV_K ** -0.5),
        "odd_w_out": nrm(ks[18], (N_ODD, CONV_WIDTH, D), CONV_WIDTH ** -0.5),
    }

def first_block(x, c, ctx, c_ctx, norm_g, ada_w, ada_b, even_w_in, even_q_norm, even_k_norm,
              even_lambda_q1, even_lambda_k1, even_lambda_q2, even_lambda_k2, even_subln,
              even_w_out, odd_w_in, odd_conv_w, odd_w_out):
    n = x.shape[1]
    ROWS = n // GRID_W
    tabs = axial_rope_tables(ROWS)
    x_lat = x
    x_ctx = ctx
    for i in range(DEPTH):
        ctx_out = need_ctx_after(i)
        shift, scale, gate = ada_params(c, ada_w[i], ada_b[i])
        shift_c, scale_c, gate_c = ada_params(c_ctx, ada_w[i], ada_b[i])
        h = modulate(x_lat, norm_g[i], shift[:, None, :], scale[:, None, :])
        if i % 2 == 0:
            e = i // 2
            w_in = even_w_in[e]
            lam_init = lambda_init_fn(i)
            lam = (jnp.exp(jnp.sum(even_lambda_q1[e].astype(jnp.float32) * even_lambda_k1[e].astype(jnp.float32)))
                   - jnp.exp(jnp.sum(even_lambda_q2[e].astype(jnp.float32) * even_lambda_k2[e].astype(jnp.float32)))
                   + lam_init)
            hc = modulate(x_ctx, norm_g[i], shift_c, scale_c)
            if ctx_out:
                proj_c = hc @ w_in
                qc, kc, vc = split_qkv(proj_c, even_q_norm[e], even_k_norm[e])
                oc = diff_attention(qc, kc, vc, lam)
                yc = even_output(proj_c, oc, even_subln[e], lam_init, even_w_out[e])
            else:
                kc, vc = split_kv(hc @ w_in[:, K0:G0], even_k_norm[e])
            proj = h @ w_in
            q, k, v = split_qkv(proj, even_q_norm[e], even_k_norm[e])
            q = apply_axial_rope(q, tabs)
            k = apply_axial_rope(k, tabs)
            k_all = jnp.concatenate([kc, k], axis=1)
            v_all = jnp.concatenate([vc, v], axis=1)
            o = diff_attention(q, k_all, v_all, lam)
            y = even_output(proj, o, even_subln[e], lam_init, even_w_out[e])
        else:
            o_i = i // 2
            y = short_conv_mixer(h @ odd_w_in[o_i], odd_conv_w[o_i], odd_w_out[o_i])
            if ctx_out:
                hc = modulate(x_ctx, norm_g[i], shift_c, scale_c)
                yc = short_conv_mixer(hc @ odd_w_in[o_i], odd_conv_w[o_i], odd_w_out[o_i])
        x_lat = x_lat + gate[:, None, :] * y
        if ctx_out:
            x_ctx = x_ctx + gate_c * yc
    return x_lat


DEPTH_2 = 1

D_RG = D_MODEL
RG_BLOCK_W = 256
RG_BLOCKS = D_RG // RG_BLOCK_W
CONV_W = 4
RG_C = 8.0
HG_EXPAND = 128
HG_HEADS = D_MODEL // HG_EXPAND
HG_DK = HG_EXPAND
HG_DV = D_MODEL // HG_HEADS
HG_CHUNK = 32
F_MIN = 1e-30
D_FF = 4 * D_MODEL
NORM_EPS = 1e-6
SPLIT_SIZES = (D_RG, D_RG, HG_HEADS * HG_DK, HG_HEADS * HG_DK, HG_HEADS * HG_DV, HG_HEADS * HG_DV, D_MODEL, D_MODEL)
D_IN = sum(SPLIT_SIZES)
SPLIT_POINTS = tuple(np.cumsum(SPLIT_SIZES)[:-1].tolist())


def rms_norm_2(x, gain):
    xf = x.astype(jnp.float32)
    y = xf * lax.rsqrt(jnp.mean(xf * xf, axis=-1, keepdims=True) + NORM_EPS)
    return (y * gain.astype(jnp.float32)).astype(x.dtype)

def causal_depthwise_conv(x, w, b):
    y = lax.conv_general_dilated(
        x, w[:, None, :].astype(x.dtype), window_strides=(1,),
        padding=((CONV_W - 1, 0),), dimension_numbers=('NWC', 'WIO', 'NWC'),
        feature_group_count=x.shape[-1])
    return y + b.astype(x.dtype)

def rg_lru(x, w_r, b_r, w_i, b_i, lam):
    B_, S_, _ = x.shape
    xf = x.astype(jnp.float32)
    xb = xf.reshape(B_, S_, RG_BLOCKS, RG_BLOCK_W)
    r = jax.nn.sigmoid(jnp.einsum('bsnj,njk->bsnk', xb, w_r.astype(jnp.float32)).reshape(B_, S_, D_RG) + b_r.astype(jnp.float32))
    i = jax.nn.sigmoid(jnp.einsum('bsnj,njk->bsnk', xb, w_i.astype(jnp.float32)).reshape(B_, S_, D_RG) + b_i.astype(jnp.float32))
    log_a = -RG_C * r * jax.nn.softplus(-lam.astype(jnp.float32))
    a = jnp.exp(log_a)
    u = jnp.sqrt(jnp.maximum(-jnp.expm1(2.0 * log_a), 0.0)) * (i * xf)

    def combine(left, right):
        a1, b1 = left
        a2, b2 = right
        return a1 * a2, a2 * b1 + b2

    _, h = lax.associative_scan(combine, (a, u), axis=1)
    return h.astype(x.dtype)

def hgrn2_chunkwise(q, k, log_f, v):
    B_, S_, H, DK = q.shape
    DV = v.shape[-1]
    n_chunks = S_ // HG_CHUNK

    def to_chunks(t):
        return t.reshape(B_, n_chunks, HG_CHUNK, H, t.shape[-1]).transpose(1, 0, 3, 2, 4)

    causal = jnp.tril(jnp.ones((HG_CHUNK, HG_CHUNK), dtype=bool))

    def step(state, chunk):
        qc, kc, lfc, vc = chunk
        cum = jnp.cumsum(lfc, axis=2)
        o_inter = jnp.einsum('bhtk,bhkv->bhtv', qc * jnp.exp(cum), state)
        rel = cum[:, :, :, None, :] - cum[:, :, None, :, :]
        decay = jnp.where(causal[:, :, None], jnp.exp(jnp.minimum(rel, 0.0)), 0.0)
        scores = jnp.einsum('bhtsk,bhsk->bhts', qc[:, :, :, None, :] * decay, kc)
        o_intra = jnp.einsum('bhts,bhsv->bhtv', scores, vc)
        last = cum[:, :, -1, :]
        k_to_end = kc * jnp.exp(jnp.minimum(last[:, :, None, :] - cum, 0.0))
        state = jnp.exp(last)[..., None] * state + jnp.einsum('bhsk,bhsv->bhkv', k_to_end, vc)
        return state, o_inter + o_intra

    state0 = jnp.zeros((B_, H, DK, DV), jnp.float32)
    _, o = lax.scan(step, state0, (to_chunks(q), to_chunks(k), to_chunks(log_f), to_chunks(v)))
    return o.transpose(1, 0, 3, 2, 4).reshape(B_, S_, H, DV)

def hybrid_mixer(h, lower_bound, w_in, conv_w, conv_b, w_r, b_r, w_i, b_i, lam, hg_norm, w_out):
    B_, S_, _ = h.shape
    proj = h @ w_in
    xa, ga, q, f, v, g, m_a, m_b = jnp.split(proj, SPLIT_POINTS, axis=-1)
    xa = causal_depthwise_conv(xa, conv_w, conv_b)
    y_a = rg_lru(xa, w_r, b_r, w_i, b_i, lam) * jax.nn.gelu(ga)
    qf = jax.nn.silu(q.astype(jnp.float32)).reshape(B_, S_, HG_HEADS, HG_DK)
    zf = f.astype(jnp.float32).reshape(B_, S_, HG_HEADS, HG_DK)
    lb = lower_bound.reshape(HG_HEADS, HG_DK)
    sig = jax.nn.sigmoid(zf)
    f_gate = lb + (1.0 - lb) * sig
    log_f = jnp.log(jnp.maximum(f_gate, F_MIN))
    kf = (1.0 - lb) * jax.nn.sigmoid(-zf)
    vf = v.astype(jnp.float32).reshape(B_, S_, HG_HEADS, HG_DV)
    o = rms_norm_2(hgrn2_chunkwise(qf, kf, log_f, vf), hg_norm)
    y_b = o.reshape(B_, S_, HG_HEADS * HG_DV).astype(h.dtype) * jax.nn.silu(g)
    y = jax.nn.sigmoid(m_a) * y_a + jax.nn.sigmoid(m_b) * y_b
    return y @ w_out

def second_inputs(seed: int = 0) -> dict:
    key = jax.random.key(seed)
    ks = jax.random.split(key, 20)
    f32 = jnp.float32
    nrm = lambda k, shape, scale: jax.random.normal(k, shape, f32) * scale
    a_c = jax.random.uniform(ks[10], (DEPTH_2, D_RG), f32, minval=0.9, maxval=0.999)
    a0 = a_c ** (1.0 / RG_C)
    lam = jnp.log(a0) - jnp.log1p(-a0)
    return {
        'x': jax.random.normal(ks[0], (BATCH, SEQ, D_MODEL), f32),
        'lb_logits': nrm(ks[1], (DEPTH_2, HG_HEADS * HG_DK), 0.1),
        'norm_mix': 1.0 + nrm(ks[2], (DEPTH_2, D_MODEL), 0.02),
        'w_in': nrm(ks[3], (DEPTH_2, D_MODEL, D_IN), D_MODEL ** -0.5),
        'conv_w': nrm(ks[4], (DEPTH_2, CONV_W, D_RG), CONV_W ** -0.5),
        'conv_b': nrm(ks[5], (DEPTH_2, D_RG), 0.02),
        'w_r': nrm(ks[6], (DEPTH_2, RG_BLOCKS, RG_BLOCK_W, RG_BLOCK_W), RG_BLOCK_W ** -0.5),
        'b_r': nrm(ks[7], (DEPTH_2, D_RG), 0.02),
        'w_i': nrm(ks[8], (DEPTH_2, RG_BLOCKS, RG_BLOCK_W, RG_BLOCK_W), RG_BLOCK_W ** -0.5),
        'b_i': nrm(ks[9], (DEPTH_2, D_RG), 0.02),
        'lam': lam,
        'hg_norm': 1.0 + nrm(ks[11], (DEPTH_2, HG_DV), 0.02),
        'w_out': nrm(ks[12], (DEPTH_2, D_MODEL, D_MODEL), D_MODEL ** -0.5),
        'norm_mlp': 1.0 + nrm(ks[13], (DEPTH_2, D_MODEL), 0.02),
        'w_up': nrm(ks[14], (DEPTH_2, D_MODEL, D_FF), D_MODEL ** -0.5),
        'w_down': nrm(ks[15], (DEPTH_2, D_FF, D_MODEL), D_FF ** -0.5),
        'norm_final': 1.0 + nrm(ks[16], (D_MODEL,), 0.02),
    }

def second_block(x, lb_logits, norm_mix, w_in, conv_w, conv_b, w_r, b_r, w_i, b_i, lam, hg_norm, w_out, norm_mlp, w_up, w_down, norm_final):
    sm = jax.nn.softmax(lb_logits.astype(jnp.float32), axis=0)
    lower_bounds = jnp.clip(jnp.cumsum(sm, axis=0) - sm[0], 0.0, 1.0)
    for l in range(DEPTH_2):
        h = rms_norm_2(x, norm_mix[l])
        x = x + hybrid_mixer(h, lower_bounds[l], w_in[l], conv_w[l], conv_b[l], w_r[l], b_r[l],
                             w_i[l], b_i[l], lam[l], hg_norm[l], w_out[l])
        h = rms_norm_2(x, norm_mlp[l])
        x = x + jnp.square(jax.nn.relu(h @ w_up[l])) @ w_down[l]
    return rms_norm_2(x, norm_final)


def setup_inputs(seed=0):
    out = dict(first_inputs(seed))
    for name, value in second_inputs(seed + 1).items():
        if name != "x":
            out[name + "_2"] = value
    return out


def reference(
    x, c, ctx, c_ctx, norm_g, ada_w, ada_b, even_w_in, even_q_norm, even_k_norm, even_lambda_q1,
    even_lambda_k1, even_lambda_q2, even_lambda_k2, even_subln, even_w_out, odd_w_in,
    odd_conv_w, odd_w_out, lb_logits_2, norm_mix_2, w_in_2, conv_w_2, conv_b_2, w_r_2, b_r_2,
    w_i_2, b_i_2, lam_2, hg_norm_2, w_out_2, norm_mlp_2, w_up_2, w_down_2, norm_final_2,
):
    x = first_block(
        x, c, ctx, c_ctx, norm_g, ada_w, ada_b, even_w_in, even_q_norm, even_k_norm,
        even_lambda_q1, even_lambda_k1, even_lambda_q2, even_lambda_k2, even_subln, even_w_out,
        odd_w_in, odd_conv_w, odd_w_out,
    )
    return second_block(
        x, lb_logits_2, norm_mix_2, w_in_2, conv_w_2, conv_b_2, w_r_2, b_r_2, w_i_2, b_i_2,
        lam_2, hg_norm_2, w_out_2, norm_mlp_2, w_up_2, w_down_2, norm_final_2,
    )


_drawn_inputs = setup_inputs


def setup_inputs(seed=0):
    import zlib

    import numpy as np

    out = dict(_drawn_inputs(seed))
    spreads = {}
    factors = {'even_q_norm': 8.0,
     'even_k_norm': 8.0,
     'even_lambda_q1': 8.0,
     'even_lambda_q2': 3.228,
     'even_subln': 6.681,
     'norm_mix_2': 7.257,
     'b_r_2': 45.131,
     'b_i_2': 35.306,
     'hg_norm_2': 24.88,
     'norm_mlp_2': 18.59,
     'norm_final_2': 7.419,
     'conv_b_2': 6.322}
    for name, (base, spread) in spreads.items():
        noise = np.random.default_rng([zlib.crc32(name.encode()), seed]).standard_normal(out[name].shape)
        drawn = base * np.exp(spread * noise) if base else spread * noise
        out[name] = __import__('jax').numpy.asarray(drawn.astype(out[name].dtype))
    for name, factor in factors.items():
        out[name] = (out[name] * factor).astype(out[name].dtype)
    return out
```

```python
import concourse.bass as bass
from concourse import mybir
import numpy as np

F32 = mybir.dt.float32
F32R = mybir.dt.float32r
I32 = mybir.dt.int32
ALU = mybir.AluOpType
ACT = mybir.ActivationFunctionType
AX = mybir.AxisListType

P = 128
D = 1024
N = 1024
NC = 256
NK = NC + N
KT = D // P
NT = N // P
GRID_W = 64
GROUPS = 4
HEADS = 4
DH = 64
HG_HEADS = 8
LEVELS = 7
EPS = 1e-6
LAM_INIT = 0.8 - 0.6 * float(np.exp(-0.3 * 0))
SCALE = DH ** -0.5
F_MIN = 1e-30
RG_C = 8.0

PARAMS1 = [("norm_g", 16), ("ada_b", 48), ("c", 8), ("c_ctx", 8), ("odd_conv_w", 24),
           ("lb_logits_2", 8), ("norm_mix_2", 8), ("even_q_norm", 1), ("even_k_norm", 1),
           ("even_subln", 1), ("hg_norm_2", 1)]
PARAMS2 = [("conv_w_2", 32), ("conv_b_2", 8), ("b_r_2", 8), ("b_i_2", 8), ("lam_2", 8),
           ("norm_mlp_2", 8), ("norm_final_2", 8), ("even_lambda_q1", 1), ("even_lambda_k1", 1),
           ("even_lambda_q2", 1), ("even_lambda_k2", 1)]
HALF_ROWS = ("even_q_norm", "even_k_norm")
LAMBDAS = ("even_lambda_q1", "even_lambda_k1", "even_lambda_q2", "even_lambda_k2")


def columns_of(params):
    at, out = 0, {}
    for name, rows in params:
        out[name] = at
        at += rows
    return out, at


COL1, N1 = columns_of(PARAMS1)
COL2, N2 = columns_of(PARAMS2)

PHASES = [("four", 4), ("q", 4), ("k", 4), ("v", 4), ("g", 8), ("eo", 8), ("oi", 32), ("oo", 8),
          ("rg", 32), ("hg", 40), ("ho", 8), ("mlp", 64)]
BASE = {}
_at = 0
for _n, _c in PHASES:
    BASE[_n] = _at
    _at += _c
UNITS = _at


def shape_tables():
    ident = np.eye(P, dtype=np.float32)
    ones = np.ones((P, P), np.float32)
    blocks = np.kron(np.eye(2), np.ones((64, 64))).astype(np.float32)
    basic = np.concatenate([ident, ones, blocks], axis=1)
    c = np.arange(P)
    ang = 2 * np.pi * ((c[:, None] * c[None, :]) % P) / P
    s = 1.0 / np.sqrt(float(N) * P)
    chan = np.concatenate([np.cos(ang) * s, np.sin(ang) * s], axis=1).astype(np.float32)
    n = np.arange(N)
    ang = 2 * np.pi * ((n[:, None] * n[None, :]) % N) / N
    token = np.stack([np.cos(ang), -np.sin(ang)]).astype(np.float32)
    half = DH // 2
    freqs = (np.float32(10000.0) ** (-np.arange(0, half, 2, dtype=np.float32) / np.float32(half))).astype(np.float32)
    d = np.arange(P) % DH
    pos = np.where((d < half)[:, None], (n // GRID_W)[None, :], (n % GRID_W)[None, :]).astype(np.float32)
    a = (pos * freqs[(d % half) % (half // 2)][:, None]).astype(np.float32).astype(np.float64)
    sign = np.where((d % half) < half // 2, -1.0, 1.0)[:, None]
    rope = np.concatenate([np.cos(a), sign * np.sin(a)], axis=1).astype(np.float32)
    masks = np.zeros((P, LEVELS, 64), np.int32)
    for lev in range(LEVELS):
        L = 1 << lev
        t = [x for x in range(P) if (x // L) % 2 == 1]
        for j, tt in enumerate(t):
            for ss in range(P):
                masks[ss, lev, j] = int(ss // (2 * L) == tt // (2 * L) and (ss // L) % 2 == 0)
    masks = masks.reshape(P, -1)
    return {"basic": basic, "chan_dft": chan, "token_dft": token, "rope": rope, "masks": masks}


SWAP16 = [i + 16 if i < 16 else i - 16 for i in range(32)]


def build(nc, I, out_dram, x_scratch):
    names = {}

    def sem(name):
        if name not in names:
            names[name] = nc.alloc_semaphore(name)
        return names[name]

    base = 16512

    def at(name, offset, shape, dt=F32):
        return nc.alloc_sbuf_tensor_at(name, [P] + list(shape), dt, offset=base + offset)

    KB = 1024
    Hh = at("Hh", 0, [KT, N], F32R)
    Hl = at("Hl", 32 * KB, [KT, N], F32R)
    Wraw = at("Wraw", 64 * KB, [2, KT, P])
    Whi = at("Whi", 72 * KB, [2, KT, P], F32R)
    Wlo = at("Wlo", 80 * KB, [2, KT, P], F32R)
    c0 = 88 * KB
    basic = at("basic", c0, [3 * P])
    ident, ones, blocks = basic[:, 0:P], basic[:, P:2 * P], basic[:, 2 * P:3 * P]
    identb = ident.rearrange("p (a t) -> p a t", a=1).to_broadcast([P, 8, P])
    P1 = at("P1", c0 + 1536, [P])
    P2 = at("P2", c0 + 2048, [P])
    M = at("M", c0 + 2560, [48, 2])
    Dv = at("Dv", c0 + 2944, [96])
    small = at("small", c0 + 3328, [64])
    cs = at("cs", c0 + 3584, [KT, 2])
    A0 = Dv[:, 0:8]
    A0c = Dv[:, 8:16]
    A1 = Dv[:, 16:24]
    ZERO = Dv[:, 24:32]
    LB = Dv[:, 32:40]
    OMLB = Dv[:, 40:48]
    SPL = Dv[:, 48:56]
    EPSC = Dv[:, 56:57]
    NLAM = Dv[:, 57:58]
    SUBG = Dv[:, 58:59]
    NSPL = Dv[:, 64:72]
    y0 = 92 * KB
    x0 = y0 + 32 * KB
    t0 = x0 + 32 * KB
    Y = at("Y", y0, [KT, N])
    X = at("X", x0, [KT, N])
    adaW = at("adaW", y0, [4, KT, 256])
    rows = at("rows", t0, [2, P])
    xs = at("xs", t0 + 1 * KB, [2, D])
    Xc = at("Xc", t0 + 9 * KB, [KT, NC])
    sq = at("sq", t0 + 17 * KB, [2, N])
    Rn = at("Rn", t0 + 25 * KB, [N])
    tn = at("tn", t0 + 1 * KB, [2, N])
    hc0 = t0 + 52992 - 16 * KB
    Hch = at("Hch", hc0, [KT, NC], F32R)
    Hcl = at("Hcl", hc0 + 8 * KB, [KT, NC], F32R)
    AB = at("AB", x0, [NT, GROUPS, 2, P])
    uf = at("uf", t0, [2, N])
    chan = at("chan", t0 + 8 * KB, [2 * P])
    piece = at("piece", t0 + 10 * KB, [8, 512])
    qT = at("qT", x0, [HEADS, N])
    kT = at("kT", x0 + 16 * KB, [HEADS, NK])
    vT = at("vT", x0 + 36 * KB, [10, 4 * P])
    s0 = x0 + 56 * KB
    qsq = at("qsq", s0, [NK])
    qR = at("qR", s0 + 5 * KB, [NK])
    rope = at("rope", y0 + 16 * KB, [2, N])
    qz = at("qz", y0 + 24 * KB, [N])
    qzs = at("qzs", y0 + 28 * KB, [N])
    prob = at("prob", 0, [2, 2, NK])
    probT = at("probT", 20 * KB, [2, 10, P])
    qs = at("qs", 30 * KB, [2, 2, P])
    acol = at("acol", 32 * KB, [2, 16])
    ocol = at("ocol", 33 * KB, [96])
    obig = at("obig", 34 * KB, [32, 2 * DH])
    osq = at("osq", 50 * KB, [32 // 4, 2 * DH])
    osc = at("osc", 54 * KB, [2, 4, P])
    cgs = at("cgs", t0, [N])
    up = at("up", t0 + 4 * KB, [N + 2])
    cv = at("cv", t0 + 9 * KB, [N])
    sg = at("sg", t0 + 13 * KB, [N])
    cv2 = at("cv2", t0 + 17 * KB, [N])
    xp = at("xp", t0, [N + 3])
    xc = at("xc", t0 + 5 * KB, [2, N])
    xch = at("xch", t0 + 13 * KB, [2, N], F32R)
    xcl = at("xcl", t0 + 21 * KB, [2, N], F32R)
    gel = at("gel", t0 + 29 * KB, [2, N])
    ra = at("ra", t0 + 37 * KB, [2, N])
    ru = at("ru", t0 + 45 * KB, [N])
    hq = at("hq", t0, [N])
    hk = at("hk", t0 + 4 * KB, [N])
    hF = at("hF", t0 + 8 * KB, [N])
    hR = at("hR", t0 + 12 * KB, [N])
    hZ = at("hZ", t0 + 16 * KB, [2, N])
    hP = at("hP", t0 + 24 * KB, [N])
    hkt = at("hkt", t0 + 28 * KB, [N])
    hvt = at("hvt", t0 + 32 * KB, [N])
    hg = at("hg", t0 + 36 * KB, [N])
    hm = at("hm", t0 + 40 * KB, [N])
    ho = at("ho", t0 + 44 * KB, [N])
    hS = at("hS", t0 + 48 * KB, [P])
    mk = at("mk", t0 + 48 * KB + 512, [LEVELS, 64], I32)
    Uh = at("Uh", y0, [KT, N], F32R)
    Ul = at("Ul", t0, [KT, N], F32R)
    ut = at("ut", t0 + 32 * KB, [2, N])
    sq2 = at("sq2", t0 + 40 * KB, [2, N])
    os_ = at("os_", t0 + 9 * KB, [2, D])
    PS = nc.alloc_psum_tensor("PS", [P, 4096], F32)

    def acc(s):
        return PS[:, s * 1024:(s + 1) * 1024]

    def bank(b, n=512, off=0):
        return PS[:, b * 512 + off:b * 512 + off + n]

    w_loaded = [sem("w_loaded0"), sem("w_loaded1")]
    raw_free = sem("raw_free")
    hi_ready, lo_ready = sem("hi_ready"), sem("lo_ready")
    w_free = sem("w_free")
    acc_ready = sem("acc_ready")
    acc_free = [sem("acc_free0"), sem("acc_free1")]

    def got(eng, i, n, b):
        eng.wait_ge(acc_ready, i * n + (b + 1))

    NORM = {"nx": 0, "nc": 1, "n1": 2, "n2": 3, "n3": 4, "n4": 5}
    SPLIT = {"eo": 0, "oo": 1, "ho": 2, "mlp": 3}

    def evacuated(eng, i, n, b):
        eng.wait_ge(acc_free[b % 2], i * (n // 2) + (b // 2 + 2))


    phase_end = sem("phase_end")
    met = {"pe": 0, "act": 0, "dve": 0}

    def rendezvous(name, eng):
        met[name] += 1
        eng.drain().then_inc(phase_end, 1)
        eng.wait_ge(phase_end, 3 * met[name])

    nW = I
    def mat(ap):
        return ap.rearrange("(k p) m -> p k m", p=P)

    w_in0 = mat(nW["even_w_in"][0])
    odd_in = mat(nW["odd_w_in"][0])
    w_in2 = mat(nW["w_in_2"][0])
    squares = {"eo": mat(nW["even_w_out"][0]), "oo": mat(nW["odd_w_out"][0]), "ho": mat(nW["w_out_2"][0])}
    w_up = mat(nW["w_up_2"][0])
    w_down = nW["w_down_2"][0].rearrange("(c k p) m -> p c k m", p=P, k=KT)
    w_r = nW["w_r_2"][0].rearrange("b (k p) m -> p b k m", p=P)
    w_i = nW["w_i_2"][0].rearrange("b (k p) m -> p b k m", p=P)
    ada = nW["ada_w"].rearrange("l (k p) m -> p l k m", p=P)

    def sp_program(sp):
        def unit_from(u, slot, dst, src):
            need = sp.snap(u + 1)
            sp.wait_ge(sem("rows_cleared"), 1)
            sp.wait_ge(lo_ready, need)
            sp.dma_start(dst, src).then_inc(w_loaded[slot], 16)

        def units(phase, n_iter, cols, m):
            n = len(cols)
            with sp.Fori(1, n_iter + 1) as i:
                for j, (off, step) in enumerate(cols):
                    col = sp.snap(i * step + (off - step))
                    unit_from(i * n + (BASE[phase] + j - n), j % 2, Wraw[:, j % 2, :, :], m[:, :, bass.ds(col, P)])

        sp.dma_start(basic[:, :], nW["basic"]).then_inc(sem("const_loaded"), 16)
        sp.wait_ge(sem("rows_cleared"), 1)
        for r, params in enumerate((PARAMS1, PARAMS2)):
            a = 0
            for name, cnt in params:
                src = nW[name]
                width = 64 if name in HALF_ROWS or name in LAMBDAS else 128
                if len(src.shape) > 1:
                    src = src.rearrange("a b c -> (a b c)" if len(src.shape) == 3 else "a b -> (a b)")
                src = src.rearrange("(r w) -> r w", w=width)
                for h in range(2 if name in HALF_ROWS else 1):
                    sp.dma_start(rows[a:a + cnt, r, h * 64:h * 64 + width], src).then_inc(sem("params_loaded"), 16)
                a += cnt
        xr = nW["x"].rearrange("b (t p) d -> p (b t) d", p=P)
        cr = nW["ctx"].rearrange("b (t p) d -> p (b t) d", p=P)
        for t in range(NT + 2):
            sp.wait_ge(sem("xs_free"), t + 1)
            sp.dma_start(xs[:, t % 2, :], xr[:, t, :] if t < NT else cr[:, t - NT, :]).then_inc(sem(f"xs_loaded{t % 2}"), 16)
            if t < 4:
                sp.dma_start(adaW[:, t, :, :], ada[:, 0, :, t * 256:(t + 1) * 256]).then_inc(sem(f"ada_loaded{t}"), 16)
        with sp.Fori(1, 6) as i:
            layer = sp.snap(i // 3)
            for s in range(4):
                col = sp.snap((i % 3) * 1024 + s * 256)
                sp.wait_ge(sem("rows_cleared"), 1)
                sp.wait_ge(sem("ada_free"), i * 4 + (s + 1))
                sp.dma_start(adaW[:, s, :, :], ada[:, bass.ds(layer, 1), :, bass.ds(col, 256)].rearrange(
                    "p l k m -> p (l k) m")).then_inc(sem(f"ada_loaded{s}"), 16)
        units("four", 2, [(0, 256), (128, 256)], w_in0)
        units("q", 2, [(512, 256), (640, 256)], w_in0)
        units("k", 2, [(1024, 256), (1152, 256)], w_in0)
        units("v", 2, [(1536, 256), (1664, 256)], w_in0)
        units("g", 4, [(2048, 256), (2176, 256)], w_in0)
        units("eo", 4, [(0, 256), (128, 256)], squares["eo"])
        units("oi", 8, [(1024, 128), (2048, 128), (3072, 128), (0, 128)], odd_in)
        units("oo", 4, [(0, 256), (128, 256)], squares["oo"])
        with sp.Fori(0, 4) as i:
            for j, off in enumerate([0, 128, 1024, 1152, None, None, 6144, 6272]):
                u = i * 8 + (BASE["rg"] + j)
                if off is None:
                    blk = sp.snap(i * 1)
                    m = (w_r, w_i)[j - 4]
                    unit_from(u, j % 2, Wraw[:, j % 2, 0:4, :].rearrange("p (k m) c -> p k (m c)", k=2),
                              m[:, bass.ds(blk, 1), :, :].rearrange("p b k m -> p (b k) m"))
                else:
                    col = sp.snap(i * 256 + off)
                    unit_from(u, j % 2, Wraw[:, j % 2, :, :], w_in2[:, :, bass.ds(col, P)])
        with sp.Fori(0, 4) as i:
            for j in range(10):
                col = sp.snap(i * 256 + ((2048, 3072, 4096, 5120, 7168)[j % 5] + 128 * (j // 5)))
                unit_from(i * 10 + (BASE["hg"] + j), j % 2, Wraw[:, j % 2, :, :], w_in2[:, :, bass.ds(col, P)])
        units("ho", 4, [(0, 256), (128, 256)], squares["ho"])
        with sp.Fori(0, 4) as c:
            for j in range(8):
                col = sp.snap(c * 1024 + j * 128)
                unit_from(c * 16 + (BASE["mlp"] + j), j % 2, Wraw[:, j % 2, :, :], w_up[:, :, bass.ds(col, P)])
            for j in range(8):
                chunk = sp.snap(c * 1)
                unit_from(c * 16 + (BASE["mlp"] + 8 + j), j % 2, Wraw[:, j % 2, :, :],
                          w_down[:, bass.ds(chunk, 1), :, j * P:(j + 1) * P].rearrange("p c k m -> p (c k) m"))
        orow = out_dram.rearrange("b (t p) d -> p (b t) d", p=P)
        for t in range(NT):
            sp.wait_ge(sem("os_ready"), t + 1)
            sp.dma_start(orow[:, t, :], os_[:, t % 2, :]).then_inc(sem(f"stored{t % 2}"), 16)
        sp.wait_ge(sem("stored0"), 16 * (NT // 2))
        sp.wait_ge(sem("stored1"), 16 * (NT // 2))

    n_params = sum(2 if n in HALF_ROWS else 1 for n, _ in PARAMS1 + PARAMS2)

    def pool_program(pool):
        def split(u, slot, tiles=KT):
            pool.wait_ge(hi_ready, u + 1)
            pool.tensor_tensor(Wlo[:, slot, 0:tiles, :], Wraw[:, slot, 0:tiles, :],
                               Whi[:, slot, 0:tiles, :].bitcast(F32), ALU.subtract).then_inc(lo_ready, 1)

        def splits(a, b):
            with pool.Fori(0, (b - a) // 2) as i:
                for s in range(2):
                    split(i * 2 + (a + s), (a + s) % 2)

        pool.sem_inc(lo_ready, 2)
        splits(0, BASE["eo"])
        pool.wait_ge(phase_end, 2 * 3)
        pool.memset(qs[:, :, :, :], 0.0)
        pool.drain()
        with pool.Fori(0, 16) as j:
            for s in range(2):
                h, c = pool.snap(j // 4), pool.snap((j % 4) * 256 + s * 128)
                pool.wait_ge(sem("qs_free"), j * 2 + (s + 1))
                for m in range(2):
                    r = slice(64 * m, 64 * m + 64)
                    pool.tensor_copy(qs[r, s, m, :].rearrange("p (a n) -> p a n", a=1), qT[r, bass.ds(h, 1), bass.ds(c, P)]).then_inc(sem("qs_ready"), 1)
                    pool.drain()
        splits(BASE["eo"], BASE["rg"])
        with pool.Fori(0, 4) as i:
            for j in range(8):
                split(i * 8 + (BASE["rg"] + j), j % 2, 4 if j in (4, 5) else KT)
        splits(BASE["hg"], UNITS)

    gate = lambda l: 24 * l + 16
    COPY, IDN, SQRT, SQUARE = ACT.Copy, ACT.Identity, ACT.Sqrt, ACT.Square

    def act_program(act):
        def split(u, slot, load, tiles=KT):
            act.wait_ge(w_loaded[slot], load)
            act.wait_ge(w_free, u + 1)
            act.activation(Whi[:, slot, 0:tiles, :], Wraw[:, slot, 0:tiles, :], COPY).then_inc(hi_ready, 1)

        def split_next(i, n, b, tiles=KT):
            b += 1
            if b < UNITS:
                split(i * n + b, b % 2, i * (8 * n) + 16 * (b // 2 + 1), tiles)

        def norm(tag, src, n, tiles_hi, shift, b0, after=None):
            if after:
                act.wait_ge(sem("x_final"), SPLIT[after] + 1)
            for k in range(KT):
                act.wait_ge(sem("sq_free"), KT * NORM[tag] + k + 1)
                act.activation(sq2[:, k % 2, 0:n] if tag == "n4" else sq[:, k % 2, 0:n], src[:, k, 0:n], SQUARE).then_inc(sem("sq_ready"), 1)
            act.wait_ge(sem("ssq_ready"), NORM[tag] + 1)
            act.activation(Rn[:, 0:n], bank(b0, n), SQRT, bias=EPSC, scale=1.0 / D).then_inc(sem("rms_root"), 1)
            if tiles_hi is None:
                return
            for k in range(KT):
                act.wait_ge(sem("scaled"), KT * NORM[tag] + k + 1)
                act.activation(tiles_hi[:, k, 0:n], tn[:, k % 2, 0:n], IDN, bias=shift(k)).then_inc(sem("norm_hi"), 1)

        def split_y(tag):
            for k in range(KT):
                act.activation(Hh[:, k, :], Y[:, k, :], COPY).then_inc(sem("y_hi"), 1)

        act.wait_ge(sem("p1_ready"), 1)
        act.activation(cs[:, :, 0], P1[:, COL1["c"]:COL1["c"] + 8], ACT.Silu).then_inc(sem("cs_ready"), 1)
        act.activation(cs[:, :, 1], P1[:, COL1["c_ctx"]:COL1["c_ctx"] + 8], ACT.Silu).then_inc(sem("cs_ready"), 1)
        act.wait_ge(sem("lb_shifted"), 1)
        act.activation(small[:, 0:8], small[:, 0:8], ACT.Exp).then_inc(sem("lb_exp"), 1)
        act.wait_ge(sem("lam_abs"), 1)
        act.activation(small[:, 32:40], small[:, 24:32], ACT.Exp, scale=-1.0).then_inc(sem("lam_exp"), 1)
        for t in range(NT + 2):
            act.wait_ge(sem("xt_ready"), t + 1)
            dst = X[:, :, t * P:(t + 1) * P] if t < NT else Xc[:, :, (t - NT) * P:(t - NT + 1) * P]
            act.activation(dst, acc(t % 2).rearrange("p (k n) -> p k n", k=KT), COPY).then_inc(sem("xt_free"), 1)
        act.drain()
        act.dma_start(x_scratch, X[:, :, :].rearrange("p k n -> p (k n)")).then_inc(sem("x_saved"), 16)
        act.wait_ge(sem("lamsum"), 1)
        act.activation(small[:, 8:10], bank(7, 2), ACT.Exp).then_inc(sem("lamexp"), 1)
        norm("nx", X, N, Hh, lambda k: M[:, k, 0:1], 4)
        norm("nc", Xc, NC, Hch, lambda k: M[:, k, 1:2], 6)
        act.dma_start(chan[:, :], nW["chan_dft"]).then_inc(sem("chan_loaded"), 16)
        split(0, 0, 16)
        rendezvous("act", act)
        with act.Fori(0, 2) as i:
            for s in range(2):
                split_next(i, 2, BASE["four"] + s)
                act.wait_ge(acc_ready, i * 2 + (s + 1))
                act.wait_ge(sem("uf_free"), i * 2 + (s + 1))
                act.activation(uf[:, s, :], acc(s), COPY).then_inc(acc_free[s], 1)
        tok = nW["token_dft"].rearrange("c (k p) n -> p c k n", p=P)
        with act.Fori(0, 2) as j:
            for q in range(16):
                col = act.snap(j * 512)
                act.wait_ge(sem("piece_free"), j * 16 + (q + 1))
                act.dma_start(piece[:, q % 8, :], tok[:, q % 2, q // 2, bass.ds(col, 512)]).then_inc(sem(f"piece_loaded{q % 8}"), 16)
        act.wait_ge(sem("fourier_free"), 3)
        act.dma_start(rope[:, :, :], nW["rope"].rearrange("p (a n) -> p a n", a=2)).then_inc(sem("rope_loaded"), 16)
        for ph, n in (("q", N), ("k", NK)):
            with act.Fori(0, 2) as i:
                for s in range(2):
                    split_next(i, 2, BASE[ph] + s)
                    act.wait_ge(acc_ready, i * 2 + (BASE[ph] + s + 1))
                    act.activation(qsq[:, 0:N], acc(s), SQUARE)
                    if ph == "k":
                        act.wait_ge(sem("ctx_ready"), i * 2 + (s + 1))
                        act.activation(qsq[:, N:NK], bank(6, NC), SQUARE)
                    act.drain().then_inc(sem("qsq_ready"), 1)
                    act.wait_ge(sem("qssq"), i * 2 + ((0 if ph == "q" else 4) + s + 1))
                    act.wait_ge(sem("qR_free"), i * 2 + ((0 if ph == "q" else 4) + s + 1))
                    act.activation(qR[:, 0:N], bank(4, N), SQRT, bias=EPSC, scale=1.0 / DH)
                    if ph == "k":
                        act.activation(qR[:, N:NK], bank(7, NC), SQRT, bias=EPSC, scale=1.0 / DH)
                    act.drain().then_inc(sem("qroot"), 1)
        with act.Fori(0, 2) as i:
            for s in range(2):
                split_next(i, 2, BASE["v"] + s)
                act.wait_ge(acc_ready, i * 2 + (BASE["v"] + s + 1))
                act.wait_ge(sem("vfm_free"), i * 2 + (s + 1))
                act.activation(qsq[:, 0:N], acc(s), COPY)
                act.wait_ge(sem("ctx_ready"), i * 2 + (4 + s + 1))
                act.activation(qsq[:, N:NK], bank(6, NC), COPY)
                act.drain().then_inc(acc_free[s], 1)
        act.wait_ge(sem("vfm_free"), 5)
        act.wait_ge(sem("qR_free"), 9)
        with act.Fori(0, 2) as i:
            for s in range(2):
                split_next(i, 2, BASE["g"] + s)
                act.wait_ge(acc_ready, i * 2 + (BASE["g"] + s + 1))
                act.wait_ge(sem("sg_free"), i * 2 + (s + 1))
                act.activation((qsq, qR)[s][:, 0:N], acc(s), ACT.Silu).then_inc(acc_free[s], 1)
        with act.Fori(0, 2) as i:
            for s in range(2):
                split_next(i, 2, BASE["g"] + 4 + s)
                act.wait_ge(acc_ready, i * 2 + (BASE["g"] + 4 + s + 1))
                act.activation(Y[:, i * 2 + (4 + s), :], acc(s), ACT.Silu).then_inc(acc_free[s], 1)
        rendezvous("act", act)
        def exps(i, s):
            act.wait_ge(sem("prob_free"), i + (s + 1))
            for m in range(2):
                act.wait_ge(sem("negmax"), i * 2 + (2 * s + m + 1))
                act.activation(prob[:, s, m, :], PS[:, 1536 * m:1536 * m + NK], ACT.Exp, bias=acol[:, s, 2 + m:3 + m],
                               scale=SCALE, accum_out=acol[:, s, 4 + m:5 + m]).then_inc(sem("exp_ready"), 1)

        def back(i, s):
            for g in range(3):
                n = 4 if g < 2 else 2
                act.wait_ge(sem("pt_psum"), i * 3 + (3 * s + g + 1))
                if g == 0:
                    act.wait_ge(sem("probT_free"), i + (s + 1))
                act.activation(probT[:, s, 4 * g:4 * g + n, :], bank(6 + g % 2, n * P).rearrange("p (t n) -> p t n", n=P),
                               COPY).then_inc(sem("pt_ready"), 1)
            act.wait_ge(sem("o_psum"), i + (s + 1))
            act.activation(obig[:, i + s, :], bank(7, P), IDN,
                           scale=acol[:, s, 6:7]).then_inc(sem("o_ready"), 1)

        exps(0, 0)
        with act.Fori(0, 15) as j:
            for s in (1, 0):
                exps(j * 2 + (0 if s else 2), s)
                back(j * 2, 1 - s)
        exps(30, 1)
        back(30, 0)
        back(30, 1)
        act.wait_ge(sem("ossq"), 1)
        act.activation(ocol[:, 32:64], ocol[:, 0:32], SQRT, bias=EPSC, scale=1.0 / (2 * DH)).then_inc(sem("oroot"), 1)
        rendezvous("act", act)
        act.dma_start(X[:, :, :].rearrange("p k n -> p (k n)"), x_scratch).then_inc(sem("x_back"), 16)
        split_y("eo")
        with act.Fori(0, 4) as i:
            for s in range(2):
                split_next(i, 2, BASE["eo"] + s)
        norm("n1", X, N, Hh, lambda k: M[:, 24 + k, 0:1], 4, "eo")
        rendezvous("act", act)
        with act.Fori(0, 8) as i:
            b = BASE["oi"]
            split_next(i, 4, b)
            act.wait_ge(acc_ready, i * 4 + (b + 1))
            act.wait_ge(sem("cgs_free"), i + 1)
            act.activation(cgs[:, :], acc(0), COPY).then_inc(acc_free[0], 1)
            split_next(i, 4, b + 1)
            split_next(i, 4, b + 2)
            act.wait_ge(acc_ready, i * 4 + (b + 3))
            act.wait_ge(sem("osg_free"), i + 1)
            act.activation(sg[:, :], acc(0), ACT.Silu).then_inc(acc_free[0], 1)
            split_next(i, 4, b + 3)
        rendezvous("act", act)
        split_y("oo")
        with act.Fori(0, 4) as i:
            for s in range(2):
                split_next(i, 2, BASE["oo"] + s)
        norm("n2", X, N, Hh, lambda k: ZERO[:, 0:1], 4, "oo")
        rendezvous("act", act)
        with act.Fori(0, 4) as i:
            b = BASE["rg"]
            for m in range(2):
                split_next(i, 8, b + m)
                got(act, i, 8, b + m)
                act.wait_ge(sem("xp_free"), i * 2 + (m + 1))
                act.activation(xp[:, 3:3 + N], acc(m), COPY).then_inc(acc_free[m], 1)
                act.wait_ge(sem("xc_ready"), i * 2 + (m + 1))
                act.activation(xch[:, m, :], xc[:, m, :], COPY).then_inc(sem("xch_ready"), 1)
            for m in range(2):
                split_next(i, 8, b + 2 + m, 4 if m == 1 else KT)
                got(act, i, 8, b + 2 + m)
                act.wait_ge(sem("scan_done"), i * 2 + (m + 1))
                act.activation(gel[:, m, :], acc(m), ACT.Gelu_apprx_tanh).then_inc(acc_free[m], 1)
            split_next(i, 8, b + 4, 4)
            got(act, i, 8, b + 4)
            act.activation(ra[:, 1, :], bank(4, N), ACT.Sigmoid, bias=P2[:, bass.ds(i * 2 + (COL2["b_r_2"] + 1), 1)]).then_inc(sem("rg_psum_read"), 1)
            act.activation(ra[:, 0, :], acc(0), ACT.Sigmoid, bias=P2[:, bass.ds(i * 2 + COL2["b_r_2"], 1)]).then_inc(acc_free[0], 1)
            split_next(i, 8, b + 5)
            got(act, i, 8, b + 5)
            act.activation(Y[:, i * 2 + 1, :], bank(6, N), ACT.Sigmoid, bias=P2[:, bass.ds(i * 2 + (COL2["b_i_2"] + 1), 1)]).then_inc(sem("rg_psum_read"), 1)
            act.activation(Y[:, i * 2, :], acc(1), ACT.Sigmoid, bias=P2[:, bass.ds(i * 2 + COL2["b_i_2"], 1)]).then_inc(acc_free[1], 1)
            for m in range(2):
                act.drain()
                act.wait_ge(sem("ru_free"), i * 2 + (m + 1))
                act.activation(ru[:, :], ra[:, m, :], ACT.Tanh, scale=NSPL[:, bass.ds(i * 2 + m, 1)])
                act.drain()
                act.activation(ra[:, m, :], ra[:, m, :], ACT.Exp, scale=SPL[:, bass.ds(i * 2 + m, 1)]).then_inc(sem("a_ready"), 1)
                act.wait_ge(sem("w_ready"), i * 2 + (m + 1))
                act.activation(ru[:, :], xp[:, 3:3 + N], SQRT).then_inc(sem("root_ready"), 1)
            for m in range(2):
                split_next(i, 8, b + 6 + m)
                got(act, i, 8, b + 6 + m)
                act.wait_ge(sem("scan_done"), i * 2 + (2 + m + 1))
                act.activation(ra[:, m, :], acc(m), ACT.Sigmoid).then_inc(acc_free[m], 1)
        act.dma_start(mk[:, :, :].rearrange("p a b -> p (a b)"), nW["masks"]).then_inc(sem("mk_loaded"), 16)
        rendezvous("act", act)
        with act.Fori(0, 4) as i:
            for s in range(2):
                b = BASE["hg"] + 5 * s
                split_next(i, 10, b)
                got(act, i, 10, b)
                act.wait_ge(sem("head_done"), i * 2 + (s + 1))
                act.activation(hq[:, :], acc(b % 2), ACT.Silu).then_inc(acc_free[b % 2], 1)
                split_next(i, 10, b + 1)
                got(act, i, 10, b + 1)
                act.activation(hF[:, :], acc((b + 1) % 2), ACT.Sigmoid)
                act.activation(hk[:, :], acc((b + 1) % 2), ACT.Sigmoid, scale=-1.0).then_inc(acc_free[(b + 1) % 2], 1)
                split_next(i, 10, b + 2)
                got(act, i, 10, b + 2)
                act.activation(ho[:, :], acc(b % 2), COPY).then_inc(acc_free[b % 2], 1)
                act.wait_ge(sem("vt_psum"), i * 2 + (s + 1))
                act.activation(hvt[:, :], bank(6, N), COPY).then_inc(sem("vt_ready"), 1)
                split_next(i, 10, b + 3)
                got(act, i, 10, b + 3)
                act.activation(hg[:, :], acc((b + 1) % 2), ACT.Silu).then_inc(acc_free[(b + 1) % 2], 1)
                split_next(i, 10, b + 4)
                got(act, i, 10, b + 4)
                act.activation(hm[:, :], acc(b % 2), ACT.Sigmoid).then_inc(acc_free[b % 2], 1)
                act.wait_ge(sem("kt_psum"), i * 2 + (s + 1))
                act.activation(hkt[:, :], bank(6, N), COPY).then_inc(sem("kt_ready"), 1)
                act.wait_ge(sem("ho_psum"), i * 2 + (s + 1))
                act.activation(hk[:, :], bank(4, N), SQUARE).then_inc(sem("hosq"), 1)
                act.wait_ge(sem("hossq"), i * 2 + (s + 1))
                act.activation(hF[:, :], bank(6, N), SQRT, bias=EPSC, scale=1.0 / P).then_inc(sem("horoot"), 1)
        rendezvous("act", act)
        split_y("ho")
        with act.Fori(0, 4) as i:
            for s in range(2):
                split_next(i, 2, BASE["ho"] + s)
        norm("n3", X, N, Hh, lambda k: ZERO[:, 0:1], 4, "ho")
        rendezvous("act", act)
        def mlp_chunk(c, last):
            for k in range(8):
                split_next(c, 16, BASE["mlp"] + k)
                got(act, c, 16, BASE["mlp"] + k)
                act.wait_ge(sem("ut_free"), c * 8 + (k + 1))
                act.activation(ut[:, k % 2, :], acc(k % 2), ACT.Relu).then_inc(acc_free[k % 2], 1)
                act.wait_ge(sem("usq_ready"), c * 8 + (k + 1))
                act.activation(Uh[:, k, :], sq2[:, k % 2, :], COPY).then_inc(sem("uh_ready"), 1)
            for k in range(8):
                if not (last and k == 7):
                    split_next(c, 16, BASE["mlp"] + 8 + k)

        with act.Fori(0, 3) as c:
            mlp_chunk(c, False)
        mlp_chunk(3, True)
        norm("n4", X, N, None, None, 4, "mlp")
        for t in range(NT):
            act.wait_ge(sem("out_psum"), t + 1)
            if t >= 2:
                act.wait_ge(sem(f"stored{t % 2}"), 16 * (t // 2))
            act.activation(os_[:, t % 2, :], acc(t % 2), COPY).then_inc(sem("os_ready"), 1)

    def dve_program(dve):
        stt, tt, ts = dve.scalar_tensor_tensor, dve.tensor_tensor, dve.tensor_scalar

        def norm(tag, src, n, hi, lo, gain, shift):
            dve.wait_ge(sem("rms_root"), NORM[tag] + 1)
            dve.reciprocal(Rn[:, 0:n], Rn[:, 0:n])
            dve.drain()
            for k in range(KT + 1):
                if k < KT:
                    dst = tn[:, k % 2, 0:n] if hi is not None else src[:, k, 0:n]
                    dve.drain()
                    stt(dst, src[:, k, 0:n], gain(k), Rn[:, 0:n], ALU.mult, ALU.mult).then_inc(sem("scaled"), 1)
                if k > 0 and hi is not None:
                    j = k - 1
                    dve.drain()
                    dve.wait_ge(sem("norm_hi"), KT * NORM[tag] + j + 1)
                    stt(lo[:, j, 0:n], tn[:, j % 2, 0:n], shift(j), hi[:, j, 0:n].bitcast(F32), ALU.add,
                        ALU.subtract).then_inc(sem("norm_lo"), 1)

        def split_y(tag):
            for k in range(KT):
                dve.wait_ge(sem("y_hi"), KT * SPLIT[tag] + k + 1)
                tt(Hl[:, k, :], Y[:, k, :], Hh[:, k, :].bitcast(F32), ALU.subtract).then_inc(sem("y_lo"), 1)

        def residual(tag, layer):
            with dve.Fori(0, 4) as i:
                for s in range(2):
                    got(dve, i, 2, BASE[tag] + s)
                    k = i * 2 + s
                    if layer is None:
                        tt(X[:, k, :], X[:, k, :], acc(s), ALU.add).then_inc(acc_free[s], 1)
                    else:
                        stt(X[:, k, :], acc(s), M[:, i * 2 + (gate(layer) + s), 0:1], X[:, k, :], ALU.mult,
                            ALU.add).then_inc(acc_free[s], 1)
            dve.drain().then_inc(sem("x_final"), 1)

        for name, n in (("m_ready", 4), ("ab_ready", 1), ("fourier_free", 1), ("qR_free", 1), ("ctx_free", 1),
                        ("v_out", 1), ("sg_free", 2), ("oT_free", 2), ("cgs_free", 1), ("osg_free", 1),
                        ("scan_done", 2), ("ru_free", 1), ("head_done", 1), ("ut_free", 2)):
            dve.sem_inc(sem(name), n)
        dve.memset(rows[:, :, :], 0.0).then_inc(sem("rows_cleared"), 1)
        dve.memset(ZERO, 0.0)
        dve.memset(EPSC, EPS)
        dve.wait_ge(sem("p_psum"), 1)
        dve.tensor_copy(P1[:, 0:N1], bank(6, N1)).then_inc(sem("p1_ready"), 1)
        dve.tensor_copy(P2[:, 0:N2], bank(6, N2, 128))
        dve.drain()
        lbl = P1[:, COL1["lb_logits_2"]:COL1["lb_logits_2"] + 8]
        tt(small[:, 0:8], lbl, lbl, ALU.subtract).then_inc(sem("lb_shifted"), 1)
        l0 = COL2["even_lambda_q1"]
        tt(small[0:64, 16:17], P2[0:64, l0:l0 + 1], P2[0:64, l0 + 1:l0 + 2], ALU.mult)
        tt(small[0:64, 17:18], P2[0:64, l0 + 2:l0 + 3], P2[0:64, l0 + 3:l0 + 4], ALU.mult)
        dve.drain().then_inc(sem("lamprod"), 1)
        lam = P2[:, COL2["lam_2"]:COL2["lam_2"] + 8]
        stt(small[:, 24:32], lam, -1.0, lam, ALU.mult, ALU.max)
        dve.drain().then_inc(sem("lam_abs"), 1)
        dve.wait_ge(sem("lam_exp"), 1)
        z, w, s2, pz = small[:, 32:40], small[:, 40:48], small[:, 48:56], small[:, 56:64]
        ts(w, z, 2.0, None, ALU.add)
        dve.drain()
        dve.reciprocal(w, w)
        dve.drain()
        tt(w, z, w, ALU.mult)
        dve.drain()
        tt(s2, w, w, ALU.mult)
        dve.drain()
        ts(pz, s2, 1.0 / 17, None, ALU.mult)
        for q in (15, 13, 11, 9, 7, 5, 3):
            dve.drain()
            stt(pz, pz, 1.0 / q, s2, ALU.add, ALU.mult)
        dve.drain()
        stt(pz, pz, 1.0, w, ALU.add, ALU.mult)
        dve.drain()
        ts(w, lam, -1.0, 0.0, ALU.mult, ALU.max)
        dve.drain()
        stt(pz, pz, 2.0, w, ALU.mult, ALU.add)
        dve.drain()
        ts(SPL, pz, -RG_C, None, ALU.mult)
        ts(NSPL, pz, RG_C, None, ALU.mult)
        sm = small[:, 0:8]
        dve.wait_ge(sem("lb_exp"), 1)
        dve.reciprocal(small[:, 24:32], sm)
        dve.drain()
        tt(sm, sm, small[:, 24:32], ALU.mult)
        dve.drain()
        tt(LB, sm, sm, ALU.subtract)
        dve.drain()
        ts(LB, LB, 0.0, 1.0, ALU.max, ALU.min)
        dve.drain()
        ts(OMLB, LB, -1.0, 1.0, ALU.mult, ALU.add)
        ts(SUBG, P1[:, COL1["even_subln"]:COL1["even_subln"] + 1], 1.0 - LAM_INIT, None, ALU.mult)
        with dve.Fori(0, 6) as i:
            for s in range(4):
                dve.wait_ge(sem("ada_psum"), i * 4 + (s + 1))
                k = i * 8 + 2 * s
                bias = P1[:, bass.ds(k + COL1["ada_b"], 2)].rearrange("p (a b) -> p a b", b=1).to_broadcast([P, 2, 2])
                tt(M[:, bass.ds(k, 2), :], bank(4 + s, 4, 256).rearrange("p (a b) -> p a b", b=2), bias, ALU.add).then_inc(sem("m_ready"), 1)
        dve.drain()
        for dst, l, c in ((A0, 0, 0), (A0c, 0, 1), (A1, 1, 0)):
            stt(dst, M[:, 24 * l + 8:24 * l + 16, c], 1.0, P1[:, COL1["norm_g"] + 8 * l:COL1["norm_g"] + 8 * l + 8], ALU.add, ALU.mult)
        dve.wait_ge(sem("lamexp"), 1)
        tt(NLAM, small[:, 9:10], small[:, 8:9], ALU.subtract)
        dve.drain()
        ts(NLAM, NLAM, -LAM_INIT, None, ALU.add)
        dve.drain()
        dve.wait_ge(sem("xt_free"), NT + 2 + 2)
        norm("nx", X, N, Hh, Hl, lambda k: A0[:, k:k + 1], lambda k: M[:, k, 0:1])
        norm("nc", Xc, NC, Hch, Hcl, lambda k: A0c[:, k:k + 1], lambda k: M[:, k, 1:2])
        dve.wait_ge(sem("x_saved"), 16)
        rendezvous("dve", dve)
        with dve.Fori(0, 2) as i:
            for s in range(2):
                dve.wait_ge(sem("chan_psum"), i * 2 + (s + 1))
                dve.tensor_copy(AB[:, :, i * 2 + s, :, :].rearrange("p t a c -> p t (a c)"),
                                bank(4, 2048).rearrange("p (t x) -> p t x", t=NT)).then_inc(sem("ab_ready"), 1)
        for j in range(2):
            dve.wait_ge(sem("fourier_psum"), j + 1)
            dve.tensor_copy(Y[:, 0:4, j * 512:(j + 1) * 512], PS[:, 0:2048].rearrange("p (g n) -> p g n", g=4)).then_inc(sem("fourier_free"), 1)
        dve.wait_ge(sem("rope_loaded"), 16)
        for ph, n, dst, off in (("q", N, qT, 0), ("k", NK, kT, NC)):
            g = P1[:, COL1[f"even_{ph}_norm"]:COL1[f"even_{ph}_norm"] + 1]
            with dve.Fori(0, 2) as i:
                for s in range(2):
                    dve.wait_ge(sem("qroot"), i * 2 + ((0 if ph == "q" else 4) + s + 1))
                    dve.reciprocal(qR[:, 0:n], qR[:, 0:n])
                    dve.drain()
                    stt(qz[:, :], acc(s), g, qR[:, 0:N], ALU.mult, ALU.mult).then_inc(acc_free[s], 1)
                    if ph == "k":
                        stt(kT[:, i * 2 + s, 0:NC], bank(6, NC), g, qR[:, N:NK], ALU.mult, ALU.mult).then_inc(sem("ctx_free"), 1)
                    dve.drain().then_inc(sem("qR_free"), 1)
                    dve.stream_shuffle(qzs[:, :], qz[:, :], SWAP16)
                    dve.drain()
                    tt(qz[:, :], qz[:, :], rope[:, 0, :], ALU.mult)
                    tt(qzs[:, :], qzs[:, :], rope[:, 1, :], ALU.mult)
                    dve.drain()
                    tt(dst[:, i * 2 + s, off:off + N], qz[:, :], qzs[:, :], ALU.add)
                    dve.drain()
        with dve.Fori(0, 2) as i:
            for s in range(2):
                h = dve.snap(i * 256 + s * 128)
                dve.wait_ge(sem("v_psum"), i * 2 + (s + 1))
                dve.tensor_copy(vT[:, 2:10, bass.ds(h, P)], bank(4, N).rearrange("p (t v) -> p t v", v=P))
                dve.tensor_copy(vT[:, 0:2, bass.ds(h, P)], bank(7, 2 * P).rearrange("p (t v) -> p t v", v=P))
                dve.drain().then_inc(sem("v_out"), 1)
        with dve.Fori(0, 2) as i:
            for s in range(2):
                evacuated(dve, i, 2, BASE["g"] + s)
                tt(Y[:, i * 2 + s, :], Y[:, i * 2 + s, :], (qsq, qR)[s][:, 0:N], ALU.mult).then_inc(sem("sg_free"), 1)
        rendezvous("dve", dve)
        def front(i, s):
            for m in range(2):
                dve.wait_ge(sem("s_psum"), i * 2 + (2 * s + m + 1))
                dve.reduce_max(acol[:, s, m:m + 1], PS[:, 1536 * m:1536 * m + NK], AX.X)
                dve.drain()
                ts(acol[:, s, 2 + m:3 + m], acol[:, s, m:m + 1], -SCALE, None, ALU.mult).then_inc(sem("negmax"), 1)

        def combine(i, s):
            dve.wait_ge(sem("exp_ready"), i * 2 + (2 * s + 2))
            dve.reciprocal(acol[:, s, 6:8], acol[:, s, 4:6])
            dve.drain()
            stt(acol[:, s, 8:9], acol[:, s, 4:5], acol[:, s, 7:8], NLAM, ALU.mult, ALU.mult)
            dve.drain()
            stt(prob[:, s, 0, :], prob[:, s, 1, :], acol[:, s, 8:9], prob[:, s, 0, :], ALU.mult, ALU.add).then_inc(sem("weights_ready"), 1)

        front(0, 0)
        combine(0, 0)
        with dve.Fori(0, 15) as j:
            for s in (1, 0):
                front(j * 2 + (0 if s else 2), s)
                combine(j * 2 + (0 if s else 2), s)
        front(30, 1)
        combine(30, 1)
        dve.wait_ge(sem("o_ready"), 32)
        for q in range(4):
            o8 = obig[:, 8 * q:8 * q + 8, :]
            tt(osq[:, :, :], o8, o8, ALU.mult)
            dve.drain()
            dve.tensor_reduce(ocol[:, 8 * q:8 * q + 8], osq[:, :, :], AX.X, ALU.add)
            dve.drain()
        dve.drain().then_inc(sem("ossq"), 1)
        dve.wait_ge(sem("oroot"), 1)
        dve.reciprocal(ocol[:, 64:96], ocol[:, 32:64])
        dve.drain()
        for b in range(8):
            dve.wait_ge(sem("osc_free"), b + 1)
            tt(osc[:, b % 2, :, :], obig[:, 4 * b:4 * b + 4, :],
               ocol[:, 64 + 4 * b:68 + 4 * b].rearrange("p (a b) -> p a b", b=1).to_broadcast([P, 4, P]), ALU.mult).then_inc(sem("osc_ready"), 1)
            dve.wait_ge(sem("oT_psum"), b + 1)
            yv = Y[:, 4 + b // 2, (b % 2) * 512:(b % 2) * 512 + 512]
            stt(yv, bank(6 + b % 2), SUBG, yv, ALU.mult, ALU.mult).then_inc(sem("oT_free"), 1)
        rendezvous("dve", dve)
        split_y("eo")
        dve.wait_ge(sem("x_back"), 16)
        residual("eo", 0)
        norm("n1", X, N, Hh, Hl, lambda k: A1[:, k:k + 1], lambda k: M[:, 24 + k, 0:1])
        rendezvous("dve", dve)
        dve.memset(up[:, :], 0.0)
        cw = COL1["odd_conv_w"]
        dve.drain()
        with dve.Fori(0, 8) as i:
            b = BASE["oi"]
            w = [P1[:, bass.ds(i + (cw + 8 * t), 1)] for t in range(3)]
            evacuated(dve, i, 4, b)
            got(dve, i, 4, b + 1)
            tt(up[:, 1:1 + N], acc(1), cgs[:, :], ALU.mult).then_inc(acc_free[1], 1)
            dve.drain().then_inc(sem("cgs_free"), 1)
            ts(cv[:, :], up[:, 0:N], w[0], None, ALU.mult)
            dve.drain()
            stt(cv2[:, :], up[:, 1:1 + N], w[1], cv[:, :], ALU.mult, ALU.add)
            dve.drain()
            stt(cv[:, :], up[:, 2:2 + N], w[2], cv2[:, :], ALU.mult, ALU.add)
            dve.drain()
            evacuated(dve, i, 4, b + 2)
            tt(cv2[:, :], cv[:, :], sg[:, :], ALU.mult)
            dve.drain().then_inc(sem("osg_free"), 1)
            got(dve, i, 4, b + 3)
            tt(Y[:, i, :], cv2[:, :], acc(1), ALU.mult).then_inc(acc_free[1], 1)
        rendezvous("dve", dve)
        split_y("oo")
        residual("oo", 1)
        norm("n2", X, N, Hh, Hl, lambda k: P1[:, COL1["norm_mix_2"] + k:COL1["norm_mix_2"] + k + 1], lambda k: ZERO[:, 0:1])
        rendezvous("dve", dve)
        dve.memset(xp[:, :], 0.0)
        dve.drain().then_inc(sem("xp_free"), 1)
        with dve.Fori(0, 4) as i:
            b = BASE["rg"]
            for m in range(2):
                w = [P2[:, bass.ds(i * 2 + (COL2["conv_w_2"] + 8 * t + m), 1)] for t in range(4)]
                cb = P2[:, bass.ds(i * 2 + (COL2["conv_b_2"] + m), 1)]
                evacuated(dve, i, 8, b + m)
                ts(xc[:, m, :], xp[:, 3:3 + N], w[3], cb, ALU.mult, ALU.add)
                for t in (2, 1, 0):
                    dve.drain()
                    ins = stt(xc[:, m, :], xp[:, t:t + N], w[t], xc[:, m, :], ALU.mult, ALU.add)
                ins.then_inc(sem("xc_ready"), 1)
                if m == 0:
                    dve.drain().then_inc(sem("xp_free"), 1)
                dve.wait_ge(sem("xch_ready"), i * 2 + (m + 1))
                tt(xcl[:, m, :], xc[:, m, :], xch[:, m, :].bitcast(F32), ALU.subtract).then_inc(sem("xcl_ready"), 1)
            for m in range(2):
                dve.drain()
                evacuated(dve, i, 8, b + 5)
                yf = Y[:, i * 2 + m, :]
                tmp = xp[:, 3:3 + N]
                dve.wait_ge(sem("a_ready"), i * 2 + (m + 1))
                tt(tmp, ra[:, m, :], ra[:, m, :], ALU.mult)
                tt(yf, yf, xc[:, m, :], ALU.mult)
                dve.drain()
                stt(tmp, tmp, 1.0, ru[:, :], ALU.add, ALU.mult).then_inc(sem("w_ready"), 1)
                dve.wait_ge(sem("root_ready"), i * 2 + (m + 1))
                tt(yf, yf, ru[:, :], ALU.mult).then_inc(sem("ru_free"), 1)
                dve.drain()
                dve.tensor_tensor_scan(tmp, ra[:, m, :], yf, 0.0, ALU.mult, ALU.add)
                dve.drain()
                tt(yf, tmp, gel[:, m, :], ALU.mult).then_inc(sem("scan_done"), 1)
            dve.drain().then_inc(sem("xp_free"), 1)
            for m in range(2):
                evacuated(dve, i, 8, b + 6 + m)
                tt(Y[:, i * 2 + m, :], Y[:, i * 2 + m, :], ra[:, m, :], ALU.mult)
            dve.drain()
        rendezvous("dve", dve)
        dve.wait_ge(sem("mk_loaded"), 16)
        with dve.Fori(0, 4) as i:
            for s in range(2):
                b = BASE["hg"] + 5 * s
                hd = i * 2 + s
                omlb, lb = OMLB[:, bass.ds(hd, 1)], LB[:, bass.ds(hd, 1)]
                dve.memset(hR[:, :], 1.0)
                evacuated(dve, i, 10, b + 1)
                ts(hF[:, :], hF[:, :], omlb, lb, ALU.mult, ALU.add)
                ts(hk[:, :], hk[:, :], omlb, None, ALU.mult).then_inc(sem("hk_ready"), 1)
                dve.drain()
                ts(hF[:, :], hF[:, :], F_MIN, None, ALU.max)
                dve.wait_ge(sem("diag_psum"), hd + 1)
                tt(hP[:, :].rearrange("p (c t) -> p c t", t=P), bank(4, N).rearrange("p (c t) -> p c t", t=P),
                   identb, ALU.mult).then_inc(sem("diag_read"), 1)
                for lev in range(LEVELS):
                    L = 1 << lev
                    v = lambda x: x.rearrange("p (b two l) -> p b two l", two=2, l=L)
                    F4, R4, Z4 = v(hF[:, :]), v(hR[:, :]), v(hZ[:, lev % 2, :])
                    dve.drain()
                    dve.wait_ge(sem("z_free"), i * 14 + (7 * s + lev + 1))
                    tt(Z4[:, :, 1, :], v(hq[:, :])[:, :, 1, :], F4[:, :, 1, :], ALU.mult)
                    tt(Z4[:, :, 0, :], v(hk[:, :])[:, :, 0, :], R4[:, :, 0, :], ALU.mult).then_inc(sem("z_ready"), 1)
                    dve.drain()
                    nb = N // (2 * L)
                    tt(R4[:, :, 0, :], R4[:, :, 0, :], F4[:, :, 1, L - 1:L].to_broadcast([P, nb, L]), ALU.mult)
                    dve.drain()
                    tt(F4[:, :, 1, :], F4[:, :, 1, :], F4[:, :, 0, L - 1:L].to_broadcast([P, nb, L]), ALU.mult)
                    dve.wait_ge(sem("mk_loaded"), 16)
                    dve.wait_ge(sem("level_psum"), i * 14 + (7 * s + lev + 1))
                    dve.copy_predicated(hP[:, :].rearrange("p (c b two l) -> p c b two l", c=8, two=2, l=L)[:, :, :, 1, :],
                                        mk[:, lev:lev + 1, :].to_broadcast([P, 8, 64]).rearrange("p c (b l) -> p c b l", l=L),
                                        bank(4 + lev % 2).rearrange("p (c b l) -> p c b l", c=8, l=L)).then_inc(sem("level_read"), 1)
                dve.drain().then_inc(sem("scores_ready"), 1)
                tt(hk[:, :], hk[:, :], hR[:, :], ALU.mult).then_inc(sem("kend_ready"), 1)
                tt(hq[:, :], hq[:, :], hF[:, :], ALU.mult)
                dve.drain()
                for c in range(1, 8):
                    dve.wait_ge(sem("kv_psum"), hd + 1)
                    Sc, kv = hR[:, c * P:(c + 1) * P], bank(6, P, (c - 1) * P)
                    if c == 1:
                        dve.tensor_copy(Sc, kv)
                    else:
                        stt(Sc, hR[:, (c - 1) * P:c * P], hF[:, c * P - 1:c * P], kv, ALU.mult, ALU.add)
                    dve.drain()
                dve.drain().then_inc(sem("states_ready"), 1)
                dve.wait_ge(sem("horoot"), hd + 1)
                dve.reciprocal(hF[:, :], hF[:, :])
                evacuated(dve, i, 10, b + 4)
                tt(hm[:, :], hm[:, :], hg[:, :], ALU.mult)
                dve.drain()
                stt(ho[:, :], bank(4, N), P1[:, COL1["hg_norm_2"]:COL1["hg_norm_2"] + 1], hF[:, :], ALU.mult, ALU.mult)
                dve.drain()
                tt(ho[:, :], ho[:, :], hm[:, :], ALU.mult)
                dve.drain()
                tt(Y[:, hd, :], Y[:, hd, :], ho[:, :], ALU.add)
                dve.drain().then_inc(sem("head_done"), 1)
        rendezvous("dve", dve)
        split_y("ho")
        residual("ho", None)
        norm("n3", X, N, Hh, Hl, lambda k: P2[:, COL2["norm_mlp_2"] + k:COL2["norm_mlp_2"] + k + 1], lambda k: ZERO[:, 0:1])
        rendezvous("dve", dve)
        with dve.Fori(0, 4) as c:
            for k in range(8):
                b = BASE["mlp"] + k
                dve.drain()
                evacuated(dve, c, 16, b)
                tt(sq2[:, k % 2, :], ut[:, k % 2, :], ut[:, k % 2, :], ALU.mult).then_inc(sem("usq_ready"), 1)
                dve.drain().then_inc(sem("ut_free"), 1)
                dve.wait_ge(sem("uh_ready"), c * 8 + (k + 1))
                tt(Ul[:, k, :], sq2[:, k % 2, :], Uh[:, k, :].bitcast(F32), ALU.subtract).then_inc(sem("ul_ready"), 1)
            for k in range(8):
                got(dve, c, 16, BASE["mlp"] + 8 + k)
                tt(X[:, k, :], X[:, k, :], acc(k % 2), ALU.add).then_inc(acc_free[k % 2], 1)
            dve.drain()
        dve.drain().then_inc(sem("x_final"), 1)
        norm("n4", X, N, None, None, lambda k: P2[:, COL2["norm_final_2"] + k:COL2["norm_final_2"] + k + 1], None)

    def pe_program(pe):
        mm = pe.matmul

        def products(i, n, b, rhs, start=0, kt=KT, first=False):
            hi, lo = rhs
            slot = b % 2
            pe.wait_ge(lo_ready, i * n + (b + 3))
            pe.wait_ge(acc_free[slot], i * (n // 2) + (b // 2 + 1))
            for h in range(2):
                c = slice(h * 512, h * 512 + 512)
                out = acc(slot)[:, c]
                for k in range(kt):
                    if first and h == 0:
                        first(k)
                    mm(out, Whi[:, slot, k, :], hi[:, k, c], start=(k == 0), stop=False)
                    mm(out, Whi[:, slot, k, :], lo[:, k, c], start=False, stop=False)
                    last = mm(out, Wlo[:, slot, k, :], hi[:, k, c], start=False, stop=(k == kt - 1))
            last.then_inc(acc_ready, 1)

        def released(ins=None):
            pe.drain().then_inc(w_free, 1)

        def unit(i, n, b, rhs=(Hh, Hl), first=False):
            products(i, n, b, rhs, first=first)
            released()

        def norm_sum(tag, n, b0, ring=None):
            ring = sq if ring is None else ring
            for k in range(KT):
                pe.wait_ge(sem("sq_ready"), KT * NORM[tag] + k + 1)
                for c in range(0, n, 512):
                    w = min(512, n - c)
                    mm(PS[:, b0 * 512 + c:b0 * 512 + c + w], ones, ring[:, k % 2, c:c + w], start=(k == 0), stop=(k == KT - 1))
                pe.drain().then_inc(sem("sq_free"), 1)
            pe.drain().then_inc(sem("ssq_ready"), 1)

        for name, n in (("xs_free", 2), ("ada_free", 4), ("xt_free", 2), ("uf_free", 2), ("piece_free", 8),
                        ("vfm_free", 1), ("qs_free", 2), ("prob_free", 2), ("probT_free", 2), ("osc_free", 2),
                        ("z_free", 2), ("sq_free", 2)):
            pe.sem_inc(sem(name), n)
        pe.sem_inc(w_free, 2)
        pe.sem_inc(acc_free[0], 1)
        pe.sem_inc(acc_free[1], 1)
        pe.wait_ge(sem("const_loaded"), 16)
        pe.wait_ge(sem("params_loaded"), 16 * n_params)
        pe.transpose(bank(6, N1), rows[0:N1, 0, :], ident[0:N1, 0:N1])
        pe.transpose(bank(6, N2, 128), rows[0:N2, 1, :], ident[0:N2, 0:N2]).then_inc(sem("p_psum"), 1)
        for t in range(NT + 2):
            pe.wait_ge(sem(f"xs_loaded{t % 2}"), 16 * (t // 2 + 1))
            pe.wait_ge(sem("xt_free"), t + 1)
            for k in range(KT):
                ins = pe.transpose(acc(t % 2)[:, k * P:(k + 1) * P], xs[:, t % 2, k * P:(k + 1) * P], ident)
            ins.then_inc(sem("xt_ready"), 1)
            pe.drain().then_inc(sem("xs_free"), 1)
        pe.wait_ge(sem("cs_ready"), 2)
        with pe.Fori(0, 6) as i:
            for s in range(4):
                pe.wait_ge(sem(f"ada_loaded{s}"), i * 16 + 16)
                pe.wait_ge(sem("m_ready"), i * 4 + (s + 1))
                for m in range(2):
                    for k in range(KT):
                        ins = mm(bank(4 + s, 2, 256 + 2 * m), adaW[:, s, k, m * P:(m + 1) * P], cs[:, k, :], start=(k == 0), stop=(k == KT - 1))
                ins.then_inc(sem("ada_psum"), 1)
                pe.drain().then_inc(sem("ada_free"), 1)
        pe.wait_ge(sem("m_ready"), 24 + 4)
        pe.wait_ge(sem("lamprod"), 1)
        mm(bank(7, 2), ones[0:64, :], small[0:64, 16:18], start=True, stop=True).then_inc(sem("lamsum"), 1)
        norm_sum("nx", N, 4)
        norm_sum("nc", NC, 6)
        rendezvous("pe", pe)
        pe.wait_ge(sem("chan_loaded"), 16)

        def chan_dft(i, s):
            pe.wait_ge(acc_free[s], i * 1 + 2)
            pe.wait_ge(sem("ab_ready"), i * 2 + (s + 1))
            for t in range(NT):
                ins = mm(bank(4 + t // 2, 256, (t % 2) * 256), uf[:, s, t * P:(t + 1) * P], chan[:, :], start=True, stop=True)
            ins.then_inc(sem("chan_psum"), 1)
            pe.drain().then_inc(sem("uf_free"), 1)

        with pe.Fori(0, 2) as i:
            for s in range(2):
                unit(i, 2, BASE["four"] + s)
                chan_dft(i, s)
        pe.wait_ge(sem("ab_ready"), 5)
        with pe.Fori(0, 2) as j:
            for q in range(16):
                pe.wait_ge(sem(f"piece_loaded{q % 8}"), j * 32 + 16 * (q // 8 + 1))
                if q == 0:
                    pe.wait_ge(sem("fourier_free"), j + 1)
                for g in range(GROUPS):
                    ins = mm(bank(g), AB[:, q // 2, g, q % 2, :], piece[:, q % 8, :], start=(q == 0), stop=(q == 15))
                if q == 15:
                    ins.then_inc(sem("fourier_psum"), 1)
                pe.drain().then_inc(sem("piece_free"), 1)
        pe.wait_ge(sem("fourier_free"), 3)
        for ph in ("q", "k", "v"):
            with pe.Fori(0, 2) as i:
                for s in range(2):
                    b = BASE[ph] + s
                    products(i, 2, b, (Hh, Hl))
                    if ph != "q":
                        pe.wait_ge(sem("ctx_free"), i * 2 + (s + 1) if ph == "k" else 5)
                        for k in range(KT):
                            mm(bank(6, NC), Whi[:, s, k, :], Hch[:, k, :], start=(k == 0), stop=False)
                            mm(bank(6, NC), Whi[:, s, k, :], Hcl[:, k, :], start=False, stop=False)
                            ins = mm(bank(6, NC), Wlo[:, s, k, :], Hch[:, k, :], start=False, stop=(k == KT - 1))
                        ins.then_inc(sem("ctx_ready"), 1)
                    released()
                    if ph != "v":
                        pe.wait_ge(sem("qsq_ready"), i * 2 + ((0 if ph == "q" else 4) + s + 1))
                        for c in range(2):
                            mm(bank(4 + c), blocks, qsq[:, c * 512:(c + 1) * 512], start=True, stop=True)
                        if ph == "k":
                            mm(bank(7, NC), blocks, qsq[:, N:NK], start=True, stop=True)
                        pe.drain().then_inc(sem("qssq"), 1)
                    else:
                        evacuated(pe, i, 2, b)
                        pe.wait_ge(sem("v_out"), i * 2 + (s + 1))
                        for t in range(10):
                            out = bank(4 + t // 4, P, (t % 4) * P) if t < 8 else bank(7, P, (t - 8) * P)
                            ins = pe.transpose(out, qsq[:, t * P:(t + 1) * P], ident)
                        ins.then_inc(sem("v_psum"), 1)
                        pe.drain().then_inc(sem("vfm_free"), 1)
        with pe.Fori(0, 4) as i:
            for s in range(2):
                unit(i, 2, BASE["g"] + s)
        rendezvous("pe", pe)

        def scores(i, s):
            h = pe.snap(i // 8)
            pe.wait_ge(sem("qs_ready"), i * 2 + (2 * s + 2))
            for m in range(2):
                if not (isinstance(i, int) and i == 0 and s == 0):
                    pe.wait_ge(sem("exp_ready"), i * 2 + (2 * s + m - 1))
                for c in range(0, NK, 512):
                    w = min(512, NK - c)
                    ins = mm(PS[:, 1536 * m + c:1536 * m + c + w].rearrange("p (a n) -> p a n", a=1), qs[:, s, m, :],
                             kT[:, bass.ds(h, 1), c:c + w], start=True, stop=True)
                ins.then_inc(sem("s_psum"), 1)
            pe.drain().then_inc(sem("qs_free"), 1)

        def outputs(i, s):
            hc = pe.snap((i // 8) * P)
            pe.wait_ge(sem("weights_ready"), i + (s + 1))
            for g in range(3):
                first = isinstance(i, int) and i == 0 and s == 0
                if g == 1 and not first:
                    pe.wait_ge(sem("o_ready"), i + s)
                elif g == 2 or not first:
                    pe.wait_ge(sem("pt_ready"), i * 3 + (3 * s + g // 2))
                for t in range(4 * g, min(4 * g + 4, 10)):
                    ins = pe.transpose(bank(6 + g % 2, P, (t % 4) * P), prob[:, s, 0, t * P:(t + 1) * P], ident)
                ins.then_inc(sem("pt_psum"), 1)
            pe.drain().then_inc(sem("prob_free"), 1)
            pe.wait_ge(sem("pt_ready"), i * 3 + (3 * s + 3))
            for t in range(10):
                ins = mm(bank(7, P), probT[:, s, t, :], vT[:, t, bass.ds(hc, P)], start=(t == 0), stop=(t == 9))
            ins.then_inc(sem("o_psum"), 1)
            pe.drain().then_inc(sem("probT_free"), 1)

        scores(0, 0)
        scores(0, 1)
        outputs(0, 0)
        with pe.Fori(1, 16) as j:
            scores(j * 2, 0)
            outputs(j * 2 - 2, 1)
            scores(j * 2, 1)
            outputs(j * 2, 0)
        outputs(30, 1)
        for b in range(8):
            pe.wait_ge(sem("osc_ready"), b + 1)
            pe.wait_ge(sem("oT_free"), b + 1)
            for t in range(4):
                ins = pe.transpose(bank(6 + b % 2, P, t * P), osc[:, b % 2, t, :], ident)
            ins.then_inc(sem("oT_psum"), 1)
            pe.drain().then_inc(sem("osc_free"), 1)
        rendezvous("pe", pe)

        def dense(ph, tag, norm_tag):
            pe.wait_ge(sem("y_lo"), KT * (SPLIT[ph] + 1))
            with pe.Fori(0, 4) as i:
                for s in range(2):
                    unit(i, 2, BASE[ph] + s)
            norm_sum(norm_tag, N, 4)

        dense("eo", "eo", "n1")
        rendezvous("pe", pe)
        with pe.Fori(0, 8) as i:
            for j in range(4):
                unit(i, 4, BASE["oi"] + j)
        rendezvous("pe", pe)
        dense("oo", "oo", "n2")
        rendezvous("pe", pe)
        with pe.Fori(0, 4) as i:
            b = BASE["rg"]
            for j in range(8):
                if j not in (4, 5):
                    unit(i, 8, b + j)
                    continue
                slot = j % 2
                pe.wait_ge(lo_ready, i * 8 + (b + j + 3))
                pe.wait_ge(acc_free[slot], i * 4 + ((b + j) // 2 + 1))
                if j == 4:
                    pe.wait_ge(sem("xcl_ready"), i * 2 + 2)
                for m in (1, 0):
                    for h in range(2):
                        c = slice(h * 512, h * 512 + 512)
                        out = (acc(slot) if m == 0 else bank(4 + 2 * slot, N))[:, c]
                        for k in range(2):
                            w = 2 * k + m
                            mm(out, Whi[:, slot, w, :], xch[:, k, c], start=(k == 0), stop=False)
                            mm(out, Whi[:, slot, w, :], xcl[:, k, c], start=False, stop=False)
                            last = mm(out, Wlo[:, slot, w, :], xch[:, k, c], start=False, stop=(k == 1))
                last.then_inc(acc_ready, 1)
                released()
        rendezvous("pe", pe)
        with pe.Fori(0, 4) as i:
            for s in range(2):
                b = BASE["hg"] + 5 * s
                hd = i * 2 + s
                unit(i, 10, b)
                unit(i, 10, b + 1)
                unit(i, 10, b + 2)
                evacuated(pe, i, 10, b + 2)
                for c in range(8):
                    ins = pe.transpose(bank(6, P, c * P), ho[:, c * P:(c + 1) * P], ident)
                ins.then_inc(sem("vt_psum"), 1)
                pe.wait_ge(sem("hk_ready"), hd + 1)
                pe.wait_ge(sem("head_done"), hd + 1)
                for c in range(8):
                    t = slice(c * P, (c + 1) * P)
                    ins = mm(bank(4, P, c * P), hk[:, t], hq[:, t], start=True, stop=True)
                ins.then_inc(sem("diag_psum"), 1)

                def level(lev):
                    L = 1 << lev
                    pe.wait_ge(sem("z_ready"), i * 14 + (7 * s + lev + 1))
                    if lev < 2:
                        pe.wait_ge(sem("diag_read"), hd + 1)
                    else:
                        pe.wait_ge(sem("level_read"), i * 14 + (7 * s + lev - 1))
                    for c in range(8):
                        z = hZ[:, lev % 2, c * P:(c + 1) * P]
                        right = z.rearrange("p (b two l) -> p b two l", two=2, l=L)[:, :, 1, :]
                        ins = mm(bank(4 + lev % 2, 64, c * 64).rearrange("p (b l) -> p b l", l=L), z, right, start=True, stop=True)
                    ins.then_inc(sem("level_psum"), 1)
                    pe.drain().then_inc(sem("z_free"), 1)

                level(0)
                level(1)
                unit(i, 10, b + 3)
                for lev in range(2, LEVELS - 1):
                    level(lev)
                unit(i, 10, b + 4)
                level(LEVELS - 1)
                pe.wait_ge(sem("kend_ready"), hd + 1)
                pe.wait_ge(sem("vt_ready"), hd + 1)
                for c in range(8):
                    ins = pe.transpose(bank(6, P, c * P), hk[:, c * P:(c + 1) * P], ident)
                ins.then_inc(sem("kt_psum"), 1)
                pe.wait_ge(sem("kt_ready"), hd + 1)
                for c in range(7):
                    t = slice(c * P, (c + 1) * P)
                    ins = mm(bank(6, P, c * P), hkt[:, t], hvt[:, t], start=True, stop=True)
                ins.then_inc(sem("kv_psum"), 1)
                pe.wait_ge(sem("states_ready"), hd + 1)
                for c in range(8):
                    t = slice(c * P, (c + 1) * P)
                    ins = mm(bank(4, P, c * P), hvt[:, t], hP[:, t], start=True, stop=(c == 0))
                    if c:
                        ins = mm(bank(4, P, c * P), hR[:, t], hq[:, t], start=False, stop=True)
                ins.then_inc(sem("ho_psum"), 1)
                pe.wait_ge(sem("hosq"), hd + 1)
                for c in range(2):
                    ins = mm(bank(6 + c), ones, hk[:, c * 512:(c + 1) * 512], start=True, stop=True)
                ins.then_inc(sem("hossq"), 1)
        rendezvous("pe", pe)
        dense("ho", "ho", "n3")
        rendezvous("pe", pe)
        with pe.Fori(0, 4) as c:
            for j in range(8):
                unit(c, 16, BASE["mlp"] + j)
            for j in range(8):
                unit(c, 16, BASE["mlp"] + 8 + j, (Uh, Ul),
                     first=(lambda k: pe.wait_ge(sem("ul_ready"), c * 8 + (k + 1))) if j == 0 else False)
        norm_sum("n4", N, 4, sq2)
        pe.wait_ge(sem("scaled"), KT * (NORM["n4"] + 1))
        for t in range(NT):
            if t >= 2:
                pe.wait_ge(sem("os_ready"), t - 1)
            for k in range(KT):
                ins = pe.transpose(acc(t % 2)[:, k * P:(k + 1) * P], X[:, k, t * P:(t + 1) * P], ident)
            ins.then_inc(sem("out_psum"), 1)

    with nc.Block() as block:
        block.sync(sp_program)
        block.gpsimd(pool_program)
        block.scalar(act_program)
        block.vector(dve_program)
        block.tensor(pe_program)


_TABLES = ("basic", "chan_dft", "token_dft", "rope", "masks")
_INS = ["x", "ctx", "ada_w", "even_w_in", "even_w_out", "odd_w_in", "odd_w_out", "w_in_2", "w_r_2", "w_i_2",
        "w_out_2", "w_up_2", "w_down_2"] + [n for n, _ in PARAMS1] + [n for n, _ in PARAMS2]


def kernel(**inputs):
    import concourse.bacc as bacc
    from concourse.bass_utils import run_bass_kernel_spmd

    nc = bacc.Bacc("TRN2", target_bir_lowering=False, num_devices=1)
    arrays, aps = {}, {}
    named = {n: inputs[n] for n in _INS}
    named.update(shape_tables())
    for name, a in named.items():
        a = np.ascontiguousarray(a)
        arrays[f"in_{name}"] = a
        aps[name] = nc.dram_tensor(f"in_{name}", a.shape, mybir.dt.from_np(a.dtype), kind="ExternalInput").ap()
    out = nc.dram_tensor("out", (1, N, D), F32, kind="ExternalOutput").ap()
    x_scratch = nc.dram_tensor("x_scratch", (P, KT * N), F32).ap()
    build(nc, aps, out, x_scratch)
    got = run_bass_kernel_spmd(nc, [arrays], core_ids=[0])
    return got.results[0]["out"]
```
